# Optimizing a Trainium2 kernel written in Bass

```python
import jax, jax.numpy as jnp
from jax import lax
import numpy as np

D_MODEL = 2048
BATCH = 1
SEQ = 256
DEPTH = 1

EPS = 1e-6
DA_HEADS = 8
DA_QK_DIM = 64
DA_V_DIM = 2 * DA_QK_DIM
ROPE_DIM = DA_QK_DIM // 4
ROPE_THETA = 500000.0
Q_BLOCK = 128
HG_HEADS = 8
HG_K_DIM = 128
HG_V_DIM = 128
HG_CHUNK = 64
DA_QK_W = DA_HEADS * 2 * DA_QK_DIM
DA_V_W = DA_HEADS * DA_V_DIM
HG_K_W = HG_HEADS * HG_K_DIM
HG_V_W = HG_HEADS * HG_V_DIM
SPLIT_SIZES = (DA_QK_W, DA_QK_W, DA_V_W, HG_K_W, HG_K_W, HG_K_W, HG_V_W, HG_V_W, D_MODEL, D_MODEL)
IN_W = sum(SPLIT_SIZES)
SPLIT_IDX = tuple(int(i) for i in np.cumsum(SPLIT_SIZES)[:-1])
PEER_HEADS = 8
PEER_N_KEYS = 128
PEER_N_EXPERTS = PEER_N_KEYS * PEER_N_KEYS
PEER_KEY_DIM = 256
PEER_HALF = PEER_KEY_DIM // 2
PEER_TOPK = 16
PEER_TOKEN_BLOCK = 128

kernel_name = "cond_hybrid_diffattn_hgrn2_peer_encoder"

def _rmsnorm(x, g):
    xf = x.astype(jnp.float32)
    y = xf * lax.rsqrt(jnp.mean(xf * xf, axis=-1, keepdims=True) + EPS)
    return (y * g.astype(jnp.float32)).astype(x.dtype)

def _modulate(x, g, shift, scale):
    return _rmsnorm(x, g) * (1.0 + scale[:, None, :]) + shift[:, None, :]

def _rope_tables(positions):
    inv = ROPE_THETA ** (-jnp.arange(0, ROPE_DIM, 2, dtype=jnp.float32) / ROPE_DIM)
    ang = positions.astype(jnp.float32)[..., None] * inv
    return jnp.cos(ang), jnp.sin(ang)

def _partial_rope(t, cos, sin):
    half = ROPE_DIM // 2
    c = cos[:, :, None, None, :].astype(t.dtype)
    s = sin[:, :, None, None, :].astype(t.dtype)
    x1, x2, rest = t[..., :half], t[..., half:ROPE_DIM], t[..., ROPE_DIM:]
    return jnp.concatenate([x1 * c - x2 * s, x2 * c + x1 * s, rest], axis=-1)

def _diff_attention(q, k, v, lam, lambda_init, subln_g):
    B, S, H, _, dk = q.shape
    nblk = S // Q_BLOCK
    q = q * (dk ** -0.5)
    qb = q.reshape(B, nblk, Q_BLOCK, H, 2, dk).transpose(1, 0, 2, 3, 4, 5)

    def block(qblk):
        s = jnp.einsum('bqhmd,bkhmd->bhmqk', qblk, k).astype(jnp.float32)
        p = jax.nn.softmax(s, axis=-1)
        p = p[:, :, 0] - lam * p[:, :, 1]
        return jnp.einsum('bhqk,bkhd->bqhd', p.astype(v.dtype), v)

    o = lax.map(block, qb)
    o = o.transpose(1, 0, 2, 3, 4).reshape(B, S, H, v.shape[-1])
    o = _rmsnorm(o, subln_g) * (1.0 - lambda_init)
    return o.reshape(B, S, H * v.shape[-1])

def _gla_chunkwise(q, k, v, log_f):
    B, S, H, dk = q.shape
    dv = v.shape[-1]
    L = HG_CHUNK
    C = S // L
    to_c = lambda t: t.reshape(B, C, L, H, t.shape[-1]).transpose(0, 3, 1, 2, 4)
    q, k, v, log_f = to_c(q), to_c(k), to_c(v), to_c(log_f)
    b = jnp.cumsum(log_f, axis=3)
    b_last = b[:, :, :, -1:, :]
    r = b[:, :, :, L // 2 - 1:L // 2, :]
    qi = q * jnp.exp(b - r)
    ki = k * jnp.exp(r - b)
    A = jnp.einsum('bhctd,bhcsd->bhcts', qi, ki)
    mask = jnp.tril(jnp.ones((L, L), dtype=bool))
    A = jnp.where(mask, A, 0.0)
    o_intra = jnp.einsum('bhcts,bhcsv->bhctv', A, v)
    U = jnp.einsum('bhcsd,bhcsv->bhcdv', k * jnp.exp(b_last - b), v)
    a = jnp.exp(b_last[:, :, :, 0, :])

    def step(state, inp):
        a_c, U_c = inp
        return a_c[..., None] * state + U_c, state

    s0 = jnp.zeros((B, H, dk, dv), jnp.float32)
    _, s_prev = lax.scan(step, s0, (jnp.moveaxis(a, 2, 0), jnp.moveaxis(U, 2, 0)))
    s_prev = jnp.moveaxis(s_prev, 0, 2)
    o_inter = jnp.einsum('bhctd,bhcdv->bhctv', q * jnp.exp(b), s_prev)
    o = o_intra + o_inter
    return o.transpose(0, 2, 3, 1, 4).reshape(B, S, H, dv)

def _layer_lower_bound(tbl, l):
    sm = jax.nn.softmax(tbl.astype(jnp.float32), axis=0)
    cum = jnp.cumsum(sm, axis=0)
    return (cum[l + 1] - cum[0]).reshape(HG_HEADS, HG_K_DIM)

def _hgrn2_gates(f_raw, lb):
    f = lb + (1.0 - lb) * jax.nn.sigmoid(f_raw)
    return 1.0 - f, jnp.log(f)

def _hgrn2(q_raw, ff_raw, fb_raw, i_raw, g_raw, lb_f, lb_b, norm_g):
    B, S, _ = q_raw.shape
    hk = lambda t: t.astype(jnp.float32).reshape(B, S, HG_HEADS, -1)
    q = jax.nn.silu(hk(q_raw))
    v = hk(i_raw)
    k_f, logf_f = _hgrn2_gates(hk(ff_raw), lb_f)
    k_b, logf_b = _hgrn2_gates(hk(fb_raw), lb_b)
    o_f = _gla_chunkwise(q, k_f, v, logf_f)
    flip = lambda t: jnp.flip(t, axis=1)
    o_b = flip(_gla_chunkwise(flip(q), flip(k_b), flip(v), flip(logf_b)))
    o = _rmsnorm(o_f + o_b, norm_g) * jax.nn.silu(hk(g_raw))
    return o.reshape(B, S, HG_V_W).astype(q_raw.dtype)

def _peer(h, wq, keys1, keys2, u, v):
    B, S, D = h.shape
    T = B * S
    t = h.reshape(T, D)
    qp = (t @ wq).reshape(T, PEER_HEADS, 2, PEER_HALF)
    s1 = jnp.einsum('thk,hnk->thn', qp[:, :, 0], keys1).astype(jnp.float32)
    s2 = jnp.einsum('thk,hnk->thn', qp[:, :, 1], keys2).astype(jnp.float32)
    v1, i1 = lax.top_k(s1, PEER_TOPK)
    v2, i2 = lax.top_k(s2, PEER_TOPK)
    cand = (v1[..., :, None] + v2[..., None, :]).reshape(T, PEER_HEADS, PEER_TOPK * PEER_TOPK)
    sc, ci = lax.top_k(cand, PEER_TOPK)
    e = (jnp.take_along_axis(i1, ci // PEER_TOPK, axis=-1) * PEER_N_KEYS
         + jnp.take_along_axis(i2, ci % PEER_TOPK, axis=-1))
    g = jax.nn.softmax(sc, axis=-1)
    nb = T // PEER_TOKEN_BLOCK
    kk = PEER_HEADS * PEER_TOPK
    xb = t.reshape(nb, PEER_TOKEN_BLOCK, D)
    eb = e.reshape(nb, PEER_TOKEN_BLOCK, kk)
    gb = g.reshape(nb, PEER_TOKEN_BLOCK, kk).astype(h.dtype)

    def blk(args):
        xt, et, gt = args
        us = jnp.take(u, et, axis=0)
        a = jax.nn.gelu(jnp.einsum('td,tkd->tk', xt, us), approximate=False) * gt
        vs = jnp.take(v, et, axis=0)
        return jnp.einsum('tk,tkd->td', a, vs)

    return lax.map(blk, (xb, eb, gb)).reshape(B, S, D)

def setup_inputs(seed: int = 0) -> dict:
    key = jax.random.key(seed)
    ks = jax.random.split(key, 26)
    f32 = jnp.float32
    nrm = lambda k, shape, s: jax.random.normal(k, shape, f32) * s
    gain = lambda k, shape: 1.0 + 0.02 * jax.random.normal(k, shape, f32)
    L, D = DEPTH, D_MODEL
    return {
        "x": nrm(ks[0], (BATCH, SEQ, D), 1.0),
        "c": nrm(ks[1], (BATCH, D), 1.0),
        "positions": jnp.broadcast_to(jnp.arange(SEQ, dtype=jnp.int32), (BATCH, SEQ)),
        "w_ada": nrm(ks[2], (L, D, 6 * D), 0.5 * D ** -0.5),
        "b_ada": nrm(ks[3], (L, 6 * D), 0.01),
        "norm1_g": gain(ks[4], (L, D)),
        "w_in": nrm(ks[5], (L, D, IN_W), D ** -0.5),
        "diff_lq1": nrm(ks[6], (L, DA_QK_DIM), 0.1),
        "diff_lk1": nrm(ks[7], (L, DA_QK_DIM), 0.1),
        "diff_lq2": nrm(ks[8], (L, DA_QK_DIM), 0.1),
        "diff_lk2": nrm(ks[9], (L, DA_QK_DIM), 0.1),
        "diff_subln_g": gain(ks[10], (L, DA_V_DIM)),
        "hgrn_lb_fwd": nrm(ks[11], (L + 1, HG_K_W), 0.1),
        "hgrn_lb_bwd": nrm(ks[12], (L + 1, HG_K_W), 0.1),
        "hgrn_norm_g": gain(ks[13], (L, HG_V_DIM)),
        "w_branch_attn": nrm(ks[14], (L, DA_V_W, D), DA_V_W ** -0.5),
        "w_branch_hgrn": nrm(ks[15], (L, HG_V_W, D), HG_V_W ** -0.5),
        "w_out": nrm(ks[16], (L, D, D), D ** -0.5),
        "norm2_g": gain(ks[17], (L, D)),
        "peer_wq": nrm(ks[18], (L, D, PEER_HEADS * PEER_KEY_DIM), D ** -0.5),
        "peer_keys1": nrm(ks[19], (L, PEER_HEADS, PEER_N_KEYS, PEER_HALF), PEER_HALF ** -0.5),
        "peer_keys2": nrm(ks[20], (L, PEER_HEADS, PEER_N_KEYS, PEER_HALF), PEER_HALF ** -0.5),
        "peer_u": nrm(ks[21], (L, PEER_N_EXPERTS, D), D ** -0.5),
        "peer_v": nrm(ks[22], (L, PEER_N_EXPERTS, D), PEER_HEADS ** -0.5),
        "final_norm_g": gain(ks[23], (D,)),
    }

def reference(x, c, positions, w_ada, b_ada, norm1_g, w_in, diff_lq1, diff_lk1, diff_lq2, diff_lk2,
              diff_subln_g, hgrn_lb_fwd, hgrn_lb_bwd, hgrn_norm_g, w_branch_attn, w_branch_hgrn,
              w_out, norm2_g, peer_wq, peer_keys1, peer_keys2, peer_u, peer_v, final_norm_g):
    B, S, D = x.shape
    cos, sin = _rope_tables(positions)
    for l in range(DEPTH):
        ada = jax.nn.silu(c) @ w_ada[l] + b_ada[l]
        shift1, scale1, gate1, shift2, scale2, gate2 = jnp.split(ada, 6, axis=-1)
        h = _modulate(x, norm1_g[l], shift1, scale1)
        parts = jnp.split(h @ w_in[l], SPLIT_IDX, axis=-1)
        da_q, da_k, da_v, hg_q, hg_ff, hg_fb, hg_i, hg_g, g_a, g_b = parts
        qa = _partial_rope(da_q.reshape(B, S, DA_HEADS, 2, DA_QK_DIM), cos, sin)
        ka = _partial_rope(da_k.reshape(B, S, DA_HEADS, 2, DA_QK_DIM), cos, sin)
        va = da_v.reshape(B, S, DA_HEADS, DA_V_DIM)
        lambda_init = 0.8 - 0.6 * float(np.exp(-0.3 * l))
        lam = (jnp.exp(jnp.sum(diff_lq1[l].astype(jnp.float32) * diff_lk1[l].astype(jnp.float32)))
               - jnp.exp(jnp.sum(diff_lq2[l].astype(jnp.float32) * diff_lk2[l].astype(jnp.float32)))
               + lambda_init)
        o_a = _diff_attention(qa, ka, va, lam, lambda_init, diff_subln_g[l])
        o_b = _hgrn2(hg_q, hg_ff, hg_fb, hg_i, hg_g,
                     _layer_lower_bound(hgrn_lb_fwd, l), _layer_lower_bound(hgrn_lb_bwd, l),
                     hgrn_norm_g[l])
        y = (jax.nn.sigmoid(g_a) * (o_a @ w_branch_attn[l])
             + jax.nn.sigmoid(g_b) * (o_b @ w_branch_hgrn[l]))
        x = x + gate1[:, None, :] * (y @ w_out[l])
        h2 = _modulate(x, norm2_g[l], shift2, scale2)
        x = x + gate2[:, None, :] * _peer(h2, peer_wq[l], peer_keys1[l], peer_keys2[l], peer_u[l], peer_v[l])
    return _rmsnorm(x, final_norm_g)


_drawn_inputs = setup_inputs


def setup_inputs(seed=0):
    import zlib

    import numpy as np

    out = dict(_drawn_inputs(seed))
    spreads = {}
    factors = {'b_ada': 5.29,
     'norm1_g': 8.0,
     'diff_lq1': 64.0,
     'diff_lk1': 64.0,
     'diff_lq2': 6.32,
     'diff_lk2': 64.0,
     'diff_subln_g': 64.0,
     'hgrn_lb_fwd': 8.0,
     'hgrn_lb_bwd': 8.0,
     'hgrn_norm_g': 21.405,
     'norm2_g': 51.49,
     'final_norm_g': 8.188}
    for name, (base, spread) in spreads.items():
        noise = np.random.default_rng([zlib.crc32(name.encode()), seed]).standard_normal(out[name].shape)
        drawn = base * np.exp(spread * noise) if base else spread * noise
        out[name] = __import__('jax').numpy.asarray(drawn.astype(out[name].dtype))
    for name, factor in factors.items():
        out[name] = (out[name] * factor).astype(out[name].dtype)
    return out
```

```python
from contextlib import ExitStack

import concourse.bass as bass
import numpy as np
from concourse import mybir

F32 = mybir.dt.float32
F32R = mybir.dt.float32r
I32 = mybir.dt.int32
U32 = mybir.dt.uint32
ACT = mybir.ActivationFunctionType
ALU = mybir.AluOpType
AX = mybir.AxisListType.X

P = 128
D = 2048
T = 256
KT = D // P
TT = T // P
EPS = 1e-6
NQ = 4
KQ = KT // NQ
HEADS = 8
L = 64
NC = T // L
TOPK = 16
NKEYS = 128
NEG = -3.0e38
LAMBDA_INIT = 0.2
ROPE = 16

FRONT_C0 = 0
MAIN_C0, MAIN_W0, MAIN_K = 32, 0, 18
BR_C0, BR_W0 = MAIN_C0 + 8 * MAIN_K, 96
WO_C0, WO_W0 = BR_C0 + 16, 112
WQ_C0, WQ_W0 = WO_C0 + 24, 128
U_C0, U_W0 = WQ_C0 + 24, 144
ROUTE_K, GATE_AT, REST_AT = 6, 48, 112
V_C0, V_W0 = U_C0 + 128, 272

C_ID, C_PERM, C_IOTA, C_SCAN, C_INV, C_SGN = 0, 128, 256, 384, 640, 641
C_W = 642


def layer(nc, a, x1_keep, s_keep, out):
    ctx = ExitStack()
    base = 16512
    top = [base]

    def place(name, shape, dt=F32, at=None):
        size = 4 * int(np.prod(shape[1:]))
        off = top[0] if at is None else at
        if at is None:
            top[0] += (size + 31) // 32 * 32
        assert off + size <= 229344, (name, off + size)
        return nc.alloc_sbuf_tensor_at(name, shape, dt, offset=off)

    sems = {}

    def S(name):
        if name not in sems:
            sems[name] = ctx.enter_context(nc.semaphore(name))
        return sems[name]

    with ctx:
        raw = place("raw", [P, 2, NQ, 512])
        whi = place("whi", [P, NQ, 512], F32R)
        wlo = place("wlo", [P, NQ, 512], F32R)
        hhi_at = top[0]
        hhi = place("hhi", [P, KT, T], F32R)
        hlo = place("hlo", [P, KT, T], F32R)
        ones = place("ones", [P, P])
        ident = place("ident", [P, P])
        iota = place("iota", [P, P])
        ada = place("ada", [P, 6, KT])
        bada = place("bada", [P, 6, KT])
        gains = place("gains", [P, 3, KT])
        a1 = place("a1", [P, KT])
        a2 = place("a2", [P, KT])
        cs = place("cs", [P, KT])
        ce = place("ce", [P, KT])
        eps = place("eps", [P, 1])
        lam = place("lam", [P, 4])
        ssq = place("ssq", [P, T])
        rstd = place("rstd", [P, T])
        sld = place("sld", [P, 2, T], at=top[0] - 8 * T)
        invs = place("invs", [P, 2])
        phase = top[0]

        xT = place("xT", [P, KT, T])
        acc = place("acc", [P, 3, D])
        oahi = place("oahi", [P, HEADS, T], F32R)
        oalo = place("oalo", [P, HEADS, T], F32R)
        obhi = place("obhi", [P, HEADS, T], F32R)
        oblo = place("oblo", [P, HEADS, T], F32R)
        sg = place("sg", [P, KT, 2, T])
        after_sg = top[0]
        ropc = place("ropc", [P, T])
        rops = place("rops", [P, T])
        perm = place("perm", [P, P])
        scanm = place("scanm", [P, T])
        vnorm = place("vnorm", [P, 2])
        lbt = place("lbt", [P, 2, 2, HEADS])
        lb = place("lb", [P, 2, HEADS])
        lbm = place("lbm", [P, 2, HEADS])
        lbs = place("lbs", [P, 2, HEADS])
        hq = place("hq", [P, T])
        he = place("he", [P, T])
        fE = place("fE", [P, 2, T])
        fF = place("fF", [P, 2, T])
        fK = place("fK", [P, 2, T])
        fM = place("fM", [P, 2, T])
        fL = place("fL", [P, 2, T])
        dec = place("dec", [P, 2, NC])
        hv = place("hv", [P, TT, P])
        vt = place("vt", [P, T])
        hg = place("hg", [P, T])
        heg = place("heg", [P, T])
        obv = heg
        kun = fK[:, :, :].rearrange("p a (b n) -> p a b n", b=2)
        atm = place("atm", [P, 2, TT, L])
        st = place("st", [P, 2, 3, P])
        on = place("on", [P, TT, P])
        qk = place("qk", [P, 2, T])
        ro = place("ro", [P, 2, T])
        pT = ro
        pr = place("pr", [P, TT, 2, T])
        va = place("va", [P, TT, P])
        oan = place("oan", [P, TT, P])
        sm = place("sm", [P, 40])
        top[0] = after_sg + 4096
        bm = place("bm", [P, 2, 2, T])
        yv = place("yv", [P, 2, T])
        sq = place("sq", [P, 2, T])
        hr = place("hr", [P, 2, KQ, T])
        top[0] = after_sg - 4 * KT * 2 * T
        xsq = place("xsq", [P, KT, T])
        posi = place("posi", [P, T], I32)
        ang = place("ang", [P, T])
        kk = place("kk", [P, T])
        lqk = place("lqk", [P, 4, 64])
        lpr = place("lpr", [P, 64])
        top[0] = phase + 4 * KT * T + 4 * 3 * D
        keys = place("keys", [P, 2, HEADS, P])
        scall = place("scall", [P, HEADS, 512])
        qp = place("qp", [P, 2, T])
        sc = place("sc", [P, 2, 2, P])
        scw = place("scw", [P, 2, 2, P])
        vals = place("vals", [P, 2, 2, TOPK])
        idx = place("idx", [P, 2, 2, TOPK], U32)
        idf = place("idf", [P, 2, 2, TOPK])
        cand = place("cand", [P, 2, TOPK, TOPK])
        candw = place("candw", [P, 2, 256])
        cv = place("cv", [P, 2, TOPK])
        ci = place("ci", [P, 2, TOPK], U32)
        cj = place("cj", [P, 2, 2, TOPK], U32)
        cjf = place("cjf", [P, 2, 2, TOPK])
        oneh = place("oneh", [P, 2, 2, 256])
        cg = place("cg", [P, 2, TOPK])
        zn = place("zn", [P, 2])
        zs = place("zs", [P, 2])
        zr = place("zr", [P, 2])
        eit = place("eit", [P, 3, TT, HEADS, TOPK])
        hr2 = place("hr2", [P, 2, KQ, T])
        gate_at = 229344 - 4 * T * P
        top[0] = phase
        egT = place("egT", [P, 3, T])
        o12 = place("o12", [P, 2, 2, 2, P])
        sgel = place("sgel", [P, 2, T])
        assert top[0] <= gate_at
        G = place("G", [P, T, P], at=gate_at)
        top[0] = phase
        av = place("av", [P, 2, T])
        ahi = place("ahi", [P, 2, T], F32R)
        alo = place("alo", [P, 2, T], F32R)
        assert top[0] <= gate_at
        top[0] = hhi_at
        x1 = place("x1", [P, KT, T])
        sqe = place("sqe", [P, 4, T])
        rstde = place("rstde", [P, T])

        ps = [ctx.enter_context(nc.psum_tensor(f"ps{i}", [P, 512], F32)) for i in range(8)]
        sc_ps = [ps[4], ps[5]]

        def u_ps(c, d):
            n = {(0, 0): 0, (2, 0): 1, (2, 1): 2, (1, 0): 0, (3, 1): 1, (1, 1): 2}[c, d]
            return ps[4 + c % 2][:, n * P:(n + 1) * P]

        raw_full = [S(f"raw_full{n}") for n in range(4)]
        hi_ready = S("hi_ready")
        split = S("split")
        pe_read = S("pe_read")

        def load(sp, c0, per, i, pos, halves):
            for half in range(2):
                sp.wait_ge(split, c0 + 0 + 3 * c0 + 4 * per * i + 4 * pos + 2 * half + 2)
                sp.dma_start(raw[:, pos % 2, 2 * half:2 * half + 2, :], halves[half])\
                  .then_inc(raw_full[2 * (pos % 2) + half], 16)

        def landed(eng, c0, per, i, pos, half):
            eng.wait_ge(raw_full[2 * (pos % 2) + half], 16 * (c0 // 2 + pos // 2 + 1) + 16 * (per // 2) * i)

        def hi(act, c0, per, i, pos, w, q):
            if q % 2 == 0:
                landed(act, c0, per, i, pos, q // 2)
            act.wait_ge(pe_read, 4 * w + q + 1)
            act.activation(whi[:, q, :], raw[:, pos % 2, q, :], ACT.Copy).then_inc(hi_ready, 1)

        def lo(dve, pos, w, q):
            dve.wait_ge(hi_ready, 4 * w + q + 1)
            dve.tensor_tensor(wlo[:, q, :], raw[:, pos % 2, q, :], whi[:, q, :].bitcast(F32), ALU.subtract)\
               .then_inc(split, 1)

        def ada_chunk(dve, c0, per, i, pos, dst, scalar, since=2):
            for half in range(2):
                landed(dve, c0, per, i, pos, half)
                dve.wait_ge(split, 4 * c0 + 4 * per * i + 4 * pos + 2 * half + (10 - 4 * since))
                d = dst[:, 1024 * half:1024 * half + 1024]
                dve.scalar_tensor_tensor(out=d, in0=raw[:, pos % 2, 2 * half:2 * half + 2, :].rearrange("p a n -> p (a n)"),
                                         scalar=scalar, in1=d, op0=ALU.mult, op1=ALU.add).then_inc(split, 2)

        def multiply(pe, c, q, out_ps, xh, xl, kt0=0, first=True, last=True):
            pe.wait_ge(split, 4 * c + q + 9)
            for k in range(KQ):
                w = slice(k * P, (k + 1) * P)
                begin, end = first and k == 0, last and k == KQ - 1
                pe.matmul(out_ps, wlo[:, q, w], xh[:, kt0 + k, :], start=begin, stop=False)
                pe.matmul(out_ps, whi[:, q, w], xl[:, kt0 + k, :], start=False, stop=False)
                mm = pe.matmul(out_ps, whi[:, q, w], xh[:, kt0 + k, :], start=False, stop=end)
            mm.then_inc(pe_read, 1)

        def multiplied(eng, w):
            eng.wait_ge(pe_read, 4 * w + 8)

        def apart(eng):
            eng.sem_inc(S("waits_passed"), 1)

        def at3(t, i):
            return t[:, bass.ds(i, 1), :].rearrange("p a n -> p (a n)")

        def at(t, i):
            v = t[:, bass.ds(i, 1)]
            return v.rearrange("p a n -> p (a n)") if len(v.shape) == 3 else v.rearrange("p a b n -> p (a b) n")

        def loop(eng, n, body):
            body(0, True)
            with eng.Fori(1, n) as i:
                body(i, False)

        w_halves = lambda t, i: [t[bass.ds(i, 1), :, 1024 * h:1024 * h + 1024].rearrange("a p n -> (a p) n") for h in range(2)]
        ada_rows = a["w_ada"].rearrange("(k p) n -> k p n", p=P)
        ada_halves = lambda k, s: [ada_rows[bass.ds(k, 1), :, s * D + 1024 * h:s * D + 1024 * h + 1024]
                                   .rearrange("a p n -> (a p) n") for h in range(2)]
        v_rows = a["v"].rearrange("(a b) d -> b a d", b=NKEYS)
        HEAD_W = [(24, 1), (32, 1), (40, 1), (48, 1), (0, 1), (8, 1), (16, 1), (56, 1), (64, 2), (80, 2), (65, 2), (81, 2)]
        HQ, FF, FB, HI, DQ, DK, DV, HG = range(8)

        def main_pos(j):
            return 3 * (j // 2) + 2 * (j % 2)

        block = ctx.enter_context(nc.Block())

        @block.sync
        def _(sp):
            def front(s, i):
                for j in range(2):
                    load(sp, FRONT_C0 + KT * s, 2, i, j, ada_halves(2 * i + j, s))

            sp.dma_start(cs[:, :], a["cT"]).then_inc(S("ld_c"), 16)
            with sp.Fori(0, 2) as i:
                front(0, i)
            for t, n in ((bada, "b_ada"), (gains, "gains"), (ident, "ident"), (iota, "iota"), (perm, "perm"),
                         (scanm, "scanm"), (posi, "posi"), (invs, "inv"), (lqk, "lqk"), (vnorm, "vnorm"), (lbt, "lbt")):
                sp.dma_start(t[:], a[n]).then_inc(S("ld_small"), 16)
            sp.dma_start(xT[:, :, :], a["xT"]).then_inc(S("ld_x"), 16)
            with sp.Fori(2, 8) as i:
                front(0, i)
            with sp.Fori(0, 8) as i:
                front(1, i)
            with sp.Fori(0, 8) as h:
                for j in range(6):
                    w0, st0 = HEAD_W[2 * j]
                    w1, st1 = HEAD_W[2 * j + 1]
                    load(sp, MAIN_C0, MAIN_K, h, 3 * j, w_halves(a["w_in"], st0 * h + w0))
                    load(sp, MAIN_C0, MAIN_K, h, 3 * j + 1, ada_halves(2 * h + j % 2, 2 + j // 2))
                    load(sp, MAIN_C0, MAIN_K, h, 3 * j + 2, w_halves(a["w_in"], st1 * h + w1))
            with sp.Fori(0, 8) as i:
                for j in range(2):
                    load(sp, BR_C0, 2, i, j, w_halves(a["w_br"], 2 * i + j))
            def with_gate2(c0, weights, k0):
                with sp.Fori(0, 4) as i:
                    for j in range(4):
                        load(sp, c0, 6, i, main_pos(j), w_halves(a[weights], 4 * i + j))
                        if j % 2 == 0:
                            load(sp, c0, 6, i, main_pos(j) + 1, ada_halves(2 * i + (k0 + j // 2), 5))

            with_gate2(WO_C0, "w_out", 0)
            sp.wait_ge(pe_read, 4 * WO_W0 + 4)
            sp.dma_start(keys[:], a["keys"]).then_inc(S("ld_keys"), 16)
            with_gate2(WQ_C0, "wq", 8)
            sp.wait_ge(S("x1_ready"), KT + 2)
            sp.dma_start(x1_keep, xT[:, :, :].rearrange("p k t -> p (k t)")).then_inc(S("x1_kept"), 16)
            with sp.Fori(0, HEADS) as i:
                for j in range(ROUTE_K):
                    load(sp, U_C0, ROUTE_K, i, j, w_halves(a["u"], ROUTE_K * i + j))
            for at0, end in ((GATE_AT, REST_AT), (REST_AT, NKEYS)):
                with sp.Fori(0, (end - at0) // 2) as i:
                    for j in range(2):
                        load(sp, U_C0 + at0, 2, i, j, w_halves(a["u"], 2 * i + (at0 + j)))
            def back(i, j, src):
                sp.wait_ge(S("a_made"), 2 * i + j + 1)
                sp.dma_start(sld[:, j, :], src).then_inc(S(f"s_back{j}"), 16)

            for j in range(2):
                load(sp, V_C0, 2, 0, j, [v_rows[j, :, 1024 * h:1024 * h + 1024] for h in range(2)])
            for j in range(2):
                sp.wait_ge(S(f"s_kept{j}"), 32)
                back(0, j, s_keep[j])
            sp.wait_ge(pe_read, 4 * V_W0 + 4)
            sp.dma_start(x1[:, :, :].rearrange("p k t -> p (k t)"), x1_keep).then_inc(S("x1_back"), 16)
            sp.wait_ge(S("s_kept0"), 16 * 65)
            sp.wait_ge(S("s_kept1"), 16 * 65)
            v_half = lambda i, j: [v_rows[bass.ds(2 * i + j, 1), :, 1024 * h:1024 * h + 1024].rearrange("a p n -> (a p) n")
                                   for h in range(2)]
            with sp.Fori(1, 64) as i:
                for j in range(2):
                    load(sp, V_C0, 2, i, j, v_half(i, j))
                    back(i, j, s_keep[bass.ds(2 * i + j, 1)].rearrange("a p t -> (a p) t"))
            for g in range(NQ):
                sp.wait_ge(S("y_ready"), g + 1)
                sp.dma_start(out[:, KQ * T * g:KQ * T * (g + 1)],
                             x1[:, KQ * g:KQ * (g + 1), :].rearrange("p k t -> p (k t)")).then_inc(S("stored"), 16)
            sp.wait_ge(S("stored"), 16 * NQ)

        @block.gpsimd
        def _(pool):
            pool.memset(ones[:, :], 1.0).then_inc(S("ones_set"), 1)
            pool.memset(eps[:, :], EPS).then_inc(S("ones_set"), 1)
            pool.memset(acc[:, 0:2, :], 0.0).then_inc(S("acc_zero"), 1)
            pool.memset(acc[:, 2, :], 0.0).then_inc(S("acc_zero"), 1)
            for n in range(2):
                pool.wait_ge(S("ada_sums"), n + 1)
                pool.memset(acc[:, n, :], 0.0).then_inc(S("acc_zero"), 1)
            with pool.Fori(0, 8) as h:
                pool.wait_ge(S("at_copied"), h + 1)
                apart(pool)
                for d in range(2):
                    for half in range(2):
                        v = atm[half * L:half * L + L, d, :, :]
                        sgn = 1 if d == 0 else -1
                        pool.affine_select(out=v, in_=v, compare_op=ALU.is_ge, fill=0.0, base=0,
                                           pattern=[[0, TT], [sgn, L]], channel_multiplier=-sgn)\
                            .then_inc(S("at_masked"), 1)
            pool.wait_ge(S("ada_sums"), 3)
            pool.memset(acc[:, 0, :], 0.0).then_inc(S("acc_zero"), 1)
            pool.memset(ssq[:, :], 0.0).then_inc(S("ssq_added"), 1)

            def add_sq(i, j):
                pool.wait_ge(S("sq_ready"), 2 * i + j + 1)
                pool.wait_ge(S("ssq_added"), 2 * i + j + 1)
                pool.tensor_tensor(ssq[:, :], ssq[:, :], sq[:, j, :], ALU.add).then_inc(S("ssq_added"), 1)

            with pool.Fori(0, 7) as i:
                add_sq(i, 0)
                add_sq(i, 1)
            add_sq(7, 0)
            with pool.Fori(0, 8) as i:
                for t in range(TT):
                    o = oneh[:, t, :, :].rearrange("p s (k j) -> p s k j", j=TOPK)
                    pool.wait_ge(S("idf_made"), i + 1)
                    pool.wait_ge(S("oneh_made"), 2 * i + t + 1)
                    pool.tensor_tensor(o, o, idf[:, t, :, :].unsqueeze(2).broadcast_to([P, 2, TOPK, TOPK]), ALU.mult)\
                        .then_inc(S("picked"), 1)
        @block.scalar
        def _(act):
            act.wait_ge(S("ld_c"), 16)
            act.activation(ce[:, :], cs[:, :], ACT.Exp, scale=-1.0).then_inc(S("ce_exp"), 1)
            act.wait_ge(S("lam_dots"), 2)
            act.activation(lam[:, 2:4], lam[:, 0:2], ACT.Exp).then_inc(S("lam_exp"), 1)
            act.wait_ge(S("lb_diff"), 1)
            act.activation(lbt[:, :, :, :], lbt[:, :, :, :], ACT.Exp).then_inc(S("lb_exp"), 1)
            act.wait_ge(S("ld_x"), 16)
            act.activation(xsq[:, :, :], xT[:, :, :], ACT.Square).then_inc(S("xsq"), 1)
            act.wait_ge(S("ang_ready"), 2)
            act.activation(rops[:, :], kk[:, :], ACT.Sin).then_inc(S("sin_done"), 1)
            act.activation(ropc[:, :], ang[:, :], ACT.Sin).then_inc(S("sin_done"), 1)
            act.wait_ge(S("xss"), 1)
            act.wait_ge(S("ones_set"), 2)
            act.activation(rstd[:, :], ps[0][:, 0:T], ACT.Sqrt, bias=eps[:, 0:1], scale=1.0 / D).then_inc(S("x_root"), 1)

            def sigmoids(h):
                gates = sg[:, bass.ds(2 * h, 2), :, :].rearrange("p a b t -> p (a b t)")
                act.wait_ge(S("evac"), 12 * h + 14)
                act.activation(gates, gates, ACT.Sigmoid).then_inc(S("gates_done"), 1)
                act.activation(heg[:, :], hg[:, :], ACT.Sigmoid).then_inc(S("g_sig"), 1)

            def attention_hi(h):
                act.wait_ge(S("oT"), h + 1)
                act.activation(at(oahi, h), ps[7][:, T:2 * T], ACT.Copy, scale=vnorm[:, 0:1]).then_inc(S("oa_hi"), 1)

            def hgrn_hi(h):
                act.wait_ge(S("obv_ready"), h + 2)
                act.activation(at(obhi, h), obv[:, :], ACT.Copy).then_inc(S("ob_hi"), 1)

            def evac(h, j, dst):
                multiplied(act, 12 * h + j)
                act.activation(dst, ps[j % 2][:, 0:T], ACT.Copy).then_inc(S("evac"), 1)

            def gate_evac(h, j):
                n = j - 8
                evac(h, j, sg[:, bass.ds(2 * h + n // 2, 1), n % 2, :].rearrange("p a t -> p (a t)"))

            def head(h, first):
                def split_hi(j, qs=range(4)):
                    for q in qs:
                        hi(act, MAIN_C0, MAIN_K, h, main_pos(j), 12 * h + j, q)

                split_hi(0)
                if first:
                    act.wait_ge(S("h1_gain"), 2)
                    act.wait_ge(S("x_normed"), 4)
                    for n in range(KT):
                        act.activation(hhi[:, n, :], xsq[:, n, :], ACT.Identity, scale=a1[:, n:n + 1],
                                       bias=ada[:, 0, n:n + 1]).then_inc(S("h1_hi"), 1)
                else:
                    gate_evac(h - 1, 11)
                    sigmoids(h - 1)
                split_hi(1, (0, 1))
                if not first:
                    attention_hi(h - 1)
                split_hi(1, (2, 3))
                multiplied(act, 12 * h + HQ)
                act.activation(he[:, :], ps[0][:, 0:T], ACT.Sigmoid).then_inc(S("q_sig"), 1)
                act.activation(hq[:, :], ps[0][:, 0:T], ACT.Copy).then_inc(S("evac"), 1)
                split_hi(2, (0, 1))
                if not first:
                    hgrn_hi(h - 1)
                split_hi(2, (2, 3))
                multiplied(act, 12 * h + FF)
                act.activation(fE[:, 0, :], ps[1][:, 0:T], ACT.Sigmoid).then_inc(S("evac"), 1)
                split_hi(3)
                multiplied(act, 12 * h + FB)
                act.activation(fE[:, 1, :], ps[0][:, 0:T], ACT.Sigmoid).then_inc(S("evac"), 1)
                split_hi(4, (0, 1))
                act.wait_ge(S("f_ready"), h + 1)
                act.activation(fF[:, :, :], fF[:, :, :], ACT.Ln).then_inc(S("logf"), 1)
                split_hi(4, (2, 3))
                evac(h, HI, vt[:, :])
                split_hi(5, (0, 1))
                act.wait_ge(S("b_diff"), 4 * h + 4)
                act.activation(fF[:, :, :], fM[:, :, :], ACT.Exp).then_inc(S("e_q"), 1)
                act.wait_ge(S("e_q"), h + 1)
                act.activation(fM[:, :, :], fM[:, :, :], ACT.Exp, scale=-1.0).then_inc(S("e_k"), 1)
                split_hi(5, (2,))
                act.activation(fL[:, :, :], fL[:, :, :], ACT.Exp).then_inc(S("e_u"), 1)
                act.activation(fE[:, :, :], fE[:, :, :], ACT.Exp).then_inc(S("e_b"), 1)
                split_hi(5, (3,))
                evac(h, DQ, qk[:, 0, :])
                act.wait_ge(S("hi_turned"), h + 1)
                act.activation(hv[:, :, :].rearrange("p a n -> p (a n)"), ps[7][:, 0:T], ACT.Copy).then_inc(S("hv_ready"), 1)
                split_hi(6)
                evac(h, DK, qk[:, 1, :])
                act.wait_ge(S("ku_turned"), h + 1)
                act.activation(kun.rearrange("p a b n -> p (a b n)"), ps[2][:, :], ACT.Copy).then_inc(S("kun_ready"), 1)
                act.wait_ge(S("at_done"), h + 1)
                act.activation(atm[:, :, :, :].rearrange("p a b n -> p (a b n)"), ps[3][:, 0:256], ACT.Copy)\
                   .then_inc(S("at_copied"), 1)
                split_hi(7)
                evac(h, DV, vt[:, :])
                split_hi(8, (0, 1))
                act.wait_ge(S("v_turned"), h + 1)
                act.activation(va[:, :, :].rearrange("p a n -> p (a n)"), ps[7][:, 0:T], ACT.Copy).then_inc(S("va_ready"), 1)
                split_hi(8, (2, 3))
                evac(h, HG, hg[:, :])
                split_hi(9, (0, 1))
                act.wait_ge(S("ho_done"), h + 1)
                for t in range(TT):
                    act.activation(on[:, t, :], ps[6][:, t * P:(t + 1) * P], ACT.Square,
                                   accum_out=sm[:, 16 + t:17 + t]).then_inc(S("ho_sq"), 1)
                act.wait_ge(S("smax"), h + 1)
                for t in range(TT):
                    for m in range(2):
                        n = 2 * t + m
                        act.activation(pr[:, t, m, :], sc_ps[m][:, t * T:(t + 1) * T], ACT.Exp, bias=sm[:, n:n + 1],
                                       scale=0.125, accum_out=sm[:, 4 + n:5 + n]).then_inc(S("p_exp"), 1)
                split_hi(9, (2, 3))
                gate_evac(h, 8)
                split_hi(10)
                act.wait_ge(S("p_turned"), h + 1)
                act.activation(pT[:, :, :].rearrange("p a n -> p (a n)"), ps[2][:, :], ACT.Copy).then_inc(S("pT_ready"), 1)
                gate_evac(h, 9)
                split_hi(11)
                act.wait_ge(S("ao_done"), h + 1)
                for t in range(TT):
                    act.activation(oan[:, t, :], ps[6][:, T + t * P:T + (t + 1) * P], ACT.Square,
                                   accum_out=sm[:, 18 + t:19 + t]).then_inc(S("ao_sq"), 1)
                act.wait_ge(S("ao_sq"), 2 * h + 2)
                act.activation(sm[:, 20:24], sm[:, 16:20], ACT.Sqrt, bias=eps[:, 0:1], scale=1.0 / P)\
                   .then_inc(S("o_root"), 1)
                gate_evac(h, 10)

            loop(act, HEADS, head)
            gate_evac(HEADS - 1, 11)
            sigmoids(HEADS - 1)
            attention_hi(HEADS - 1)
            hgrn_hi(HEADS - 1)

            def y_hi(n_done, slot, n):
                act.wait_ge(S("y_ready_raw"), n_done)
                act.activation(at(hhi, n), yv[:, slot, :], ACT.Copy).then_inc(S("y_hi"), 1)

            def branch(i, first):
                for j in range(2):
                    for q in range(NQ):
                        hi(act, BR_C0, 2, i, j, BR_W0 + 2 * i + j, q)
                    if j == 1:
                        y_hi(2 * i + 1, 0, 2 * i)
                    elif not first:
                        y_hi(2 * i, 1, 2 * i - 1)
            loop(act, 8, branch)

            def x1_sq(n_done, slot, n, n_added):
                act.wait_ge(S("x1_ready"), n_done + 2)
                act.wait_ge(S("ssq_added"), n_added)
                act.activation(sq[:, slot, :], at(xT, n), ACT.Square).then_inc(S("sq_ready"), 1)

            def w_out(i, first):
                for j in range(4):
                    for q in range(NQ):
                        if first and j == 0 and q == 3:
                            y_hi(16, 1, KT - 1)
                        hi(act, WO_C0, 6, i, main_pos(j), WO_W0 + 4 * i + j, q)
                    if not (first and j == 0):
                        x1_sq(4 * i + j, (j - 1) % 2, 4 * i + j - 1, 4 * i + j)
            loop(act, 4, w_out)
            for q in range(NQ):
                if q == 3:
                    x1_sq(16, 1, KT - 1, KT - 1)
                hi(act, WQ_C0, 6, 0, 0, WQ_W0, q)
            act.wait_ge(S("x1_ss"), 1)
            act.activation(rstd[:, :], ps[2][:, 0:T], ACT.Sqrt, bias=eps[:, 0:1], scale=1.0 / D).then_inc(S("x1_root"), 1)
            def copy_query(n_w, j, n_scores):
                multiplied(act, n_w)
                act.wait_ge(S("sc_done"), n_scores)
                act.activation(qp[:, j, :], ps[j][:, 0:T], ACT.Copy).then_inc(S("qp_ready"), 1)

            def copy_scores(n):
                act.wait_ge(S("sc_done"), n + 2)
                act.activation(at3(scall, n), ps[2][:, :], ACT.Copy).then_inc(S("sc_kept"), 1)

            def query(i, first):
                for g in range(2):
                    n = 2 * i + g
                    if not (first and g == 0):
                        for q in range(NQ):
                            hi(act, WQ_C0, 6, i, 3 * g, WQ_W0 + 2 * n, q)
                        copy_query(WQ_W0 + 2 * n - 1, 1, n)
                    for q in range(NQ):
                        hi(act, WQ_C0, 6, i, 3 * g + 2, WQ_W0 + 2 * n + 1, q)
                        if not (first and g == 0) and q == 1:
                            copy_scores(n - 1)
                    copy_query(WQ_W0 + 2 * n, 0, n + 1)
            act.wait_ge(S("ada_read"), 5)
            for n in range(KT):
                act.wait_ge(S("h2_normed"), n + 1)
                act.activation(hhi[:, n, :], hr2[:, (n // KQ) % 2, n % KQ, :], ACT.Identity,
                               bias=ada[:, 3, n:n + 1]).then_inc(S("h2_hi"), 1)
            loop(act, 4, query)
            copy_query(WQ_W0 + 15, 1, 8)
            copy_scores(7)

            def gelu(at0, per, i, j):
                slot = (j - 1) % 2
                n = at0 + j - 1 + per * i
                pair = (at0 + j - 1 - slot) // 2 + (per // 2) * i
                multiplied(act, U_W0 + n)
                act.wait_ge(S(f"s_kept{slot}"), 16 * pair + 16)
                act.activation(sgel[:, slot, :], ps[slot][:, 0:T], ACT.Gelu).then_inc(S("s_gelu"), 1)
                return n, slot

            def keep(n, slot):
                act.wait_ge(S("s_gelu"), n + 3)
                dst = s_keep[n] if isinstance(n, int) else s_keep[bass.ds(n, 1)].rearrange("a p t -> (a p) t")
                act.dma_start(dst, sgel[:, slot, :]).then_inc(S(f"s_kept{slot}"), 16)

            def route(i, first):
                act.wait_ge(S("sc_used"), i + 1)
                act.wait_ge(S("sc_kept"), HEADS + 1)
                act.activation(sc[:, :, :, :].rearrange("p a b n -> p (a b n)"), at3(scall, i), ACT.Copy)\
                   .then_inc(S("sc_ready"), 1)
                for j in range(ROUTE_K):
                    for q in range(NQ):
                        hi(act, U_C0, ROUTE_K, i, j, U_W0 + ROUTE_K * i + j, q)
                        if 4 * j + q == 13:
                            act.wait_ge(S("zn_ready"), 2 * i + 2)
                            for t in range(TT):
                                act.activation(cg[:, t, :], cv[:, t, :], ACT.Exp, bias=zn[:, t:t + 1],
                                               accum_out=zs[:, t:t + 1]).then_inc(S("cg_exp"), 1)
                    if not (first and j == 0):
                        keep(*gelu(0, ROUTE_K, i, j))

            act.sem_inc(S("s_kept0"), 16)
            act.sem_inc(S("s_kept1"), 16)
            loop(act, HEADS, route)
            act.wait_ge(S("x1_kept"), 16)
            act.wait_ge(S("eg_turned"), 1)
            act.activation(egT[:, 0:2, :].rearrange("p a n -> p (a n)"), ps[3][:, :], ACT.Copy).then_inc(S("egT_ready"), 1)
            act.activation(egT[:, 2, :], ps[4][:, 0:T], ACT.Copy).then_inc(S("egT_ready"), 1)

            def gate_copy(i, g):
                act.wait_ge(S("g_made"), 4 * i + g + 3)
                dst = G[:, bass.ds(8 * i + 2 * g, 2), :].rearrange("p t n -> p (t n)")
                act.activation(dst, ps[4 + g % 2][:, 0:256], ACT.Copy).then_inc(S("g_copied"), 1)

            def gates_chunks(i, first):
                for j in range(2):
                    for q in range(NQ):
                        hi(act, U_C0 + GATE_AT, 2, i, j, U_W0 + GATE_AT + 2 * i + j, q)
                        if q % 2 == 1 and j == 1:
                            gate_copy(i, q // 2)
                        elif q % 2 == 1 and not first:
                            gate_copy(i - 1, 2 + q // 2)
                    keep(*gelu(GATE_AT, 2, i, j))
            gate_bodies = (REST_AT - GATE_AT) // 2
            loop(act, gate_bodies, gates_chunks)
            gate_copy(gate_bodies - 1, 2)
            gate_copy(gate_bodies - 1, 3)
            with act.Fori(0, (NKEYS - REST_AT) // 2) as i:
                for j in range(2):
                    for q in range(NQ):
                        hi(act, U_C0 + REST_AT, 2, i, j, U_W0 + REST_AT + 2 * i + j, q)
                    keep(*gelu(REST_AT, 2, i, j))
            keep(*gelu(NKEYS, 2, 0, 0))

            def table_v(i):
                for j in range(2):
                    hi(act, V_C0, 2, i, j, V_W0 + 2 * i + j, 0)
                    hi(act, V_C0, 2, i, j, V_W0 + 2 * i + j, 1)
                    act.wait_ge(S("a_made"), 2 * i + j + 3)
                    act.activation(ahi[:, j, :], av[:, j, :], ACT.Copy).then_inc(S("a_hi"), 1)
                    hi(act, V_C0, 2, i, j, V_W0 + 2 * i + j, 2)
                    hi(act, V_C0, 2, i, j, V_W0 + 2 * i + j, 3)
            with act.Fori(0, 64) as i:
                table_v(i)
            for n in range(KT):
                act.wait_ge(S("x2_ready"), n + 1)
                if n >= 4:
                    act.wait_ge(S("sqe_added"), n - 3)
                act.activation(sqe[:, n % 4, :], x1[:, n, :], ACT.Square).then_inc(S("sqe_ready"), 1)
                act.wait_ge(S("sqe_ready"), n + 1)
                act.activation(x1[:, n, :], x1[:, n, :], ACT.Copy, scale=gains[:, 2, n:n + 1]).then_inc(S("x2_scaled"), 1)
            act.wait_ge(S("sqe_added"), KT)
            act.activation(rstde[:, :], ps[0][:, 0:T], ACT.Sqrt, bias=eps[:, 0:1], scale=1.0 / D).then_inc(S("x2_root"), 1)

        @block.tensor
        def _(pe):
            def column_sums(s, col, bank, n):
                for k in range(KT):
                    mm = pe.matmul(ps[bank][:, 16 * n + k:16 * n + k + 1], acc[:, col, k * P:(k + 1) * P], ones[:, 0:1],
                                   start=True, stop=True)
                mm.then_inc(S("ada_sums"), 1)

            pe.sem_inc(pe_read, 4)
            pe.wait_ge(S("ones_set"), 2)
            pe.wait_ge(S("xsq"), 1)
            for k in range(KT):
                mm = pe.matmul(ps[0][:, 0:T], ones[:, :], xsq[:, k, :], start=(k == 0), stop=(k == KT - 1))
            mm.then_inc(S("xss"), 1)
            for n in range(2):
                pe.wait_ge(split, 4 * KT * (n + 1) + 8)
                column_sums(n, n, 1 + n, 0)
            pe.wait_ge(S("x_root"), 1)
            pe.wait_ge(S("ada_read"), 2)
            pe.wait_ge(S("at_zero"), 1)

            def outputs_back(h):
                pe.wait_ge(S("on_ready"), 4 * h + 4)
                pe.wait_ge(S("va_ready"), h + 1)
                for k, src in enumerate((on, oan)):
                    for t in range(TT):
                        mm = pe.transpose(ps[7][:, k * T + t * P:k * T + (t + 1) * P], src[:, t, :], ident[:, :])
                mm.then_inc(S("oT"), 1)

            def head(h, first):
                w = 12 * h

                def chunk(j, qs=range(4)):
                    c = MAIN_C0 + MAIN_K * h + main_pos(j)
                    if 0 in qs:
                        pe.wait_ge(S("evac"), w + j + 1)
                    for q in qs:
                        if first and j == 0:
                            pe.wait_ge(S("h1_lo"), q + 1)
                        multiply(pe, c, q, ps[j % 2][:, 0:T], hhi, hlo, kt0=KQ * q, first=q == 0, last=q == 3)

                def turn_values(name):
                    for t in range(TT):
                        mm = pe.transpose(ps[7][:, t * P:(t + 1) * P], vt[:, t * P:(t + 1) * P], ident[:, :])
                    mm.then_inc(S(name), 1)

                chunk(0, (0, 1))
                if not first:
                    outputs_back(h - 1)
                chunk(0, (2, 3))
                for j in range(1, 5):
                    chunk(j)
                pe.wait_ge(S("evac"), w + HI + 3)
                pe.wait_ge(S("obv_ready"), h + 1)
                turn_values("hi_turned")
                chunk(5)
                pe.wait_ge(S("hg_fac"), 5 * h + 5)
                for d in range(2):
                    for t in range(TT):
                        n = 2 * t + d
                        mm = pe.transpose(ps[2][:, n * P:(n + 1) * P], fL[:, d, t * P:(t + 1) * P], ident[:, :])
                mm.then_inc(S("ku_turned"), 1)
                for d in range(2):
                    for c in range(NC):
                        t, half = c // 2, (c % 2) * L
                        for s in range(2):
                            s0 = c * L + s * L // 2
                            lo_t, hi_t = (s * L // 2, L) if d == 0 else (0, (s + 1) * L // 2)
                            mm = pe.matmul(ps[3][half + s * L // 2:half + (s + 1) * L // 2,
                                                 d * P + t * L + lo_t:d * P + t * L + hi_t],
                                           fM[:, d, s0:s0 + L // 2], fF[:, d, c * L + lo_t:c * L + hi_t],
                                           start=True, stop=True, skip_group_check=True)
                mm.then_inc(S("at_done"), 1)
                chunk(6, (0, 1))
                pe.wait_ge(S("evac"), w + DK + 3)
                pe.wait_ge(S("hv_ready"), h + 1)
                pe.matmul(ps[7][:, :], perm[:, :], qk[:, :, :].rearrange("p a n -> p (a n)"), start=True, stop=True)\
                  .then_inc(S("rot_done"), 1)
                chunk(6, (2, 3))
                pe.wait_ge(S("kun_ready"), h + 1)
                for d in range(2):
                    for n in range(3):
                        c = n if d == 0 else NC - 1 - n
                        t, half = c // 2, (c % 2) * L
                        mm = pe.matmul(u_ps(c, d), kun[half:half + L, t, d, :], hv[half:half + L, t, :],
                                       start=True, stop=True, skip_group_check=True)
                mm.then_inc(S("u_done"), 1)
                chunk(7, (0, 1))
                pe.wait_ge(S("evac"), w + DV + 3)
                pe.wait_ge(S("roped"), h + 1)
                turn_values("v_turned")
                chunk(7, (2, 3))
                pe.wait_ge(S("at_masked"), 4 * h + 4)
                pe.wait_ge(S("st_ready"), 6 * h + 6)
                apart(pe)
                for c in range(NC):
                    t, half = c // 2, (c % 2) * L
                    o = ps[6][half:half + L, t * P:(t + 1) * P]
                    for d in range(2):
                        pe.matmul(o, atm[half:half + L, d, t, :], hv[half:half + L, t, :], start=(d == 0), stop=False,
                                  skip_group_check=True)
                    for d in range(2):
                        n = c if d == 0 else NC - 1 - c
                        if n > 0:
                            mm = pe.matmul(o, fE[:, d, c * L:(c + 1) * L], st[:, d, n - 1, :], start=False,
                                           stop=(d == 1 or c == NC - 1), skip_group_check=True)
                mm.then_inc(S("ho_done"), 1)
                for t in range(TT):
                    for m in range(2):
                        mm = pe.matmul(sc_ps[m][:, t * T:(t + 1) * T], qk[m * 64:m * 64 + 64, 0, t * P:(t + 1) * P],
                                       qk[m * 64:m * 64 + 64, 1, :], start=True, stop=True, skip_group_check=True)
                mm.then_inc(S("scores"), 1)
                chunk(8)
                chunk(9)
                pe.wait_ge(S("p_ready"), 2 * h + 2)
                for k in range(TT):
                    for t in range(TT):
                        mm = pe.transpose(ps[2][:, k * T + t * P:k * T + (t + 1) * P], pr[:, t, 0, k * P:(k + 1) * P],
                                          ident[:, :])
                mm.then_inc(S("p_turned"), 1)
                chunk(10)
                pe.wait_ge(S("pT_ready"), h + 1)
                pe.wait_ge(S("ho_sq"), 2 * h + 2)
                for t in range(TT):
                    for k in range(TT):
                        mm = pe.matmul(ps[6][:, T + t * P:T + (t + 1) * P], pT[:, k, t * P:(t + 1) * P], va[:, k, :],
                                       start=(k == 0), stop=(k == TT - 1))
                mm.then_inc(S("ao_done"), 1)
                chunk(11)

            loop(pe, HEADS, head)
            outputs_back(HEADS - 1)

            pe.wait_ge(split, 4 * BR_C0 + 8)
            column_sums(2, 0, 2, 0)
            column_sums(4, 2, 2, 1)
            pe.wait_ge(S("evac"), 98)
            pe.wait_ge(S("ob_lo"), HEADS)
            with pe.Fori(0, 8) as i:
                for j in range(2):
                    pe.wait_ge(S("z_read"), 2 * i + j + 1)
                    for q in range(NQ):
                        xh, xl = (oahi, oalo) if q < 2 else (obhi, oblo)
                        multiply(pe, BR_C0 + 2 * i + j, q, ps[j][:, (q // 2) * T:(q // 2 + 1) * T], xh, xl,
                                 kt0=KQ * (q % 2), first=q % 2 == 0, last=q % 2 == 1)
            def w_out(i, first):
                for j in range(4):
                    pe.wait_ge(S("x1_ready"), 4 * i + j + 1)
                    for q in range(NQ):
                        if first and j == 0:
                            pe.wait_ge(S("y_lo"), KQ * q + KQ)
                        multiply(pe, WO_C0 + 6 * i + main_pos(j), q, ps[j % 2][:, 0:T], hhi, hlo, kt0=KQ * q,
                                 first=q == 0, last=q == 3)
            loop(pe, 4, w_out)
            pe.wait_ge(S("ssq_added"), KT)
            pe.matmul(ps[2][:, 0:T], ones[:, :], ssq[:, :], start=True, stop=False)
            pe.wait_ge(S("sq_ready"), KT)
            pe.matmul(ps[2][:, 0:T], ones[:, :], sq[:, 1, :], start=False, stop=True).then_inc(S("x1_ss"), 1)
            column_sums(3, 1, 3, 0)

            pe.wait_ge(S("x1_ready"), KT + 2)

            def scores(n):
                pe.wait_ge(S("qp_ready"), 2 * n + 4)
                pe.wait_ge(S("sc_kept"), n + 1)
                for t in range(TT):
                    for m in range(2):
                        key = keys[:, m, bass.ds(n, 1), :].rearrange("p a n -> p (a n)")
                        mm = pe.matmul(ps[2][:, (2 * t + m) * P:(2 * t + m + 1) * P], qp[:, m, t * P:(t + 1) * P], key,
                                       start=True, stop=True, skip_group_check=True)
                mm.then_inc(S("sc_done"), 1)

            pe.wait_ge(S("x1_root"), 1)

            def query(i, first):
                for j in range(4):
                    n = 2 * i + j // 2
                    pe.wait_ge(S("qp_ready"), 4 * i + j + 1)
                    for q in range(NQ):
                        if first and j == 0:
                            pe.wait_ge(S("h2_lo"), KQ * q + KQ)
                        multiply(pe, WQ_C0 + 6 * i + main_pos(j), q, ps[j % 2][:, 0:T], hhi, hlo, kt0=KQ * q,
                                 first=q == 0, last=q == 3)
                    if j % 2 == 0 and not (first and j == 0):
                        scores(n - 1)
            pe.wait_ge(S("ld_keys"), 16)
            loop(pe, 4, query)
            pe.wait_ge(split, 4 * U_C0 + 8)
            column_sums(5, 0, 3, 0)
            scores(7)
            pe.wait_ge(S("qp_ready"), 18)

            def table_u(at0, per, i, j, q):
                n = at0 + per * i + j
                if q == 0:
                    pe.wait_ge(S("s_gelu"), n + 1)
                multiply(pe, U_C0 + n, q, ps[j % 2][:, 0:T], hhi, hlo, kt0=KQ * q, first=q == 0, last=q == 3)

            with pe.Fori(0, HEADS) as i:
                for j in range(ROUTE_K):
                    for q in range(NQ):
                        table_u(0, ROUTE_K, i, j, q)
            pe.wait_ge(S("eit_ready"), 6 * HEADS)
            for n in range(3):
                for t in range(TT):
                    o = ps[3][:, n * T + t * P:n * T + (t + 1) * P] if n < 2 else ps[4][:, t * P:(t + 1) * P]
                    mm = pe.transpose(o, eit[:, n, t, :, :].rearrange("p h k -> p (h k)"), ident[:, :])
            mm.then_inc(S("eg_turned"), 1)
            with pe.Fori(0, (REST_AT - GATE_AT) // 2) as i:
                for j in range(2):
                    for q in range(NQ):
                        table_u(GATE_AT, 2, i, j, q)
                        if q in (1, 3):
                            g = 2 * j + q // 2
                            pe.wait_ge(S("onehots"), 16 * i + 4 * g + 4)
                            pe.wait_ge(S("g_copied"), 4 * i + g + 1)
                            for t in range(2):
                                mm = pe.matmul(ps[4 + g % 2][:, t * P:(t + 1) * P], o12[:, g % 2, 0, t, :],
                                               o12[:, g % 2, 1, t, :], start=True, stop=True, skip_group_check=True)
                            mm.then_inc(S("g_made"), 1)
            with pe.Fori(0, (NKEYS - REST_AT) // 2) as i:
                for j in range(2):
                    for q in range(NQ):
                        table_u(REST_AT, 2, i, j, q)

            pe.wait_ge(S("s_gelu"), 130)
            pe.wait_ge(S("g_copied"), 130)

            def table_v(i, first):
                for j in range(2):
                    pe.wait_ge(S("a_lo"), 2 * i + j + 1)
                    for q in range(NQ):
                        pe.wait_ge(split, 4 * V_C0 + 8 * i + 4 * j + q + 9)
                        for k in range(KQ):
                            n = KQ * q + k
                            o = ps[n // 2][:, (n % 2) * T:(n % 2 + 1) * T]
                            w = slice(k * P, (k + 1) * P)
                            pe.matmul(o, wlo[:, q, w], ahi[:, j, :], start=first and j == 0 and n % 2 == 0, stop=False,
                                      skip_group_check=True)
                            pe.matmul(o, whi[:, q, w], alo[:, j, :], start=False, stop=False, skip_group_check=True)
                            mm = pe.matmul(o, whi[:, q, w], ahi[:, j, :], start=False, stop=True, skip_group_check=True)
                        mm.then_inc(pe_read, 1)
            loop(pe, 64, table_v)
            pe.wait_ge(S("x2_ready"), 2)
            for n in range(KT):
                pe.wait_ge(S("sqe_ready"), n + 1)
                mm = pe.matmul(ps[0][:, 0:T], ones[:, :], sqe[:, n % 4, :], start=n == 0, stop=n == KT - 1)
                mm.then_inc(S("sqe_added"), 1)

        @block.vector
        def _(dve):
            dve.sem_inc(split, 8)
            for name, n in (("evac", 2), ("obv_ready", 1), ("z_read", 2), ("x1_ready", 2), ("qp_ready", 2),
                            ("sc_done", 1), ("sc_used", 1), ("sc_kept", 1), ("s_gelu", 2), ("g_made", 2),
                            ("g_copied", 2), ("a_made", 2)):
                dve.sem_inc(S(name), n)

            dve.memset(ps[3][:, 0:T], 0.0).then_inc(S("at_zero"), 1)
            dve.wait_ge(S("ce_exp"), 1)
            dve.tensor_scalar(ce[:, :], ce[:, :], 1.0, None, ALU.add).then_inc(S("cs_step"), 1)
            dve.wait_ge(S("cs_step"), 1)
            dve.reciprocal(ce[:, :], ce[:, :]).then_inc(S("cs_step"), 1)
            dve.wait_ge(S("cs_step"), 2)
            dve.tensor_tensor(cs[:, :], cs[:, :], ce[:, :], ALU.mult).then_inc(S("cs_step"), 1)
            def front(s, n0, n1):
                with dve.Fori(n0, n1) as i:
                    for j in range(2):
                        ada_chunk(dve, FRONT_C0 + KT * s, 2, i, j, acc[:, s, :], cs[:, bass.ds(2 * i + j, 1)], since=1)

            dve.wait_ge(S("acc_zero"), 1)
            dve.wait_ge(S("cs_step"), 3)
            front(0, 0, 4)
            dve.wait_ge(S("ld_small"), 16 * 11)
            for n in range(2):
                if n:
                    dve.wait_ge(S("lam_dots"), 1)
                dve.tensor_tensor_reduce(lpr[:, :], lqk[:, 2 * n, :], lqk[:, 2 * n + 1, :], 1.0, 0.0, ALU.mult, ALU.add,
                                         lam[:, n:n + 1]).then_inc(S("lam_dots"), 1)
            dve.tensor_tensor(lbs[:, :, :], lbt[:, :, 0, :], lbt[:, :, 1, :], ALU.max).then_inc(S("lb_step"), 1)
            dve.wait_ge(S("lb_step"), 1)
            dve.tensor_tensor(lbt[:, :, :, :], lbt[:, :, :, :], lbs[:, :, :].unsqueeze(2).broadcast_to([P, 2, 2, HEADS]),
                              ALU.subtract).then_inc(S("lb_diff"), 1)
            dve.wait_ge(S("lb_exp"), 1)
            dve.tensor_tensor(lbs[:, :, :], lbt[:, :, 0, :], lbt[:, :, 1, :], ALU.add).then_inc(S("lb_step"), 1)
            dve.wait_ge(S("lb_step"), 2)
            dve.reciprocal(lbs[:, :, :], lbs[:, :, :]).then_inc(S("lb_step"), 1)
            dve.wait_ge(S("lb_step"), 3)
            dve.tensor_tensor(lbt[:, :, :, :], lbt[:, :, :, :], lbs[:, :, :].unsqueeze(2).broadcast_to([P, 2, 2, HEADS]),
                              ALU.mult).then_inc(S("lb_step"), 1)
            dve.wait_ge(S("lb_step"), 4)
            dve.tensor_tensor(lbs[:, :, :], lbt[:, :, 0, :], lbt[:, :, 1, :], ALU.add).then_inc(S("lb_step"), 1)
            dve.wait_ge(S("lb_step"), 5)
            dve.tensor_tensor(lb[:, :, :], lbs[:, :, :], lbt[:, :, 0, :], ALU.subtract).then_inc(S("lb_step"), 1)
            dve.wait_ge(S("lb_step"), 6)
            dve.tensor_scalar(lbm[:, :, :], lb[:, :, :], -1.0, 1.0, ALU.mult, ALU.add).then_inc(S("lb_step"), 1)
            dve.wait_ge(S("lam_exp"), 1)
            dve.tensor_scalar(lam[:, 0:1], lam[:, 3:4], lam[:, 2:3], -LAMBDA_INIT, ALU.subtract, ALU.add)\
               .then_inc(S("lam_ready"), 1)
            dve.tensor_scalar(vnorm[:, 0:1], vnorm[:, 0:1], 1.0 - LAMBDA_INIT, None, ALU.mult).then_inc(S("lam_ready"), 1)
            front(0, 4, 6)
            n_ang = [0]

            def ang_step(ins):
                n_ang[0] += 1
                ins.then_inc(S("ang_step"), 1)
                dve.wait_ge(S("ang_step"), n_ang[0])
            two_pi = 2 * np.pi
            c1 = 6.28125
            c2 = float(np.float32(np.round((two_pi - c1) * 2 ** 20) / 2 ** 20))
            c3 = float(np.float32(two_pi - c1 - c2))
            pi = 3.1415925
            ang_step(dve.tensor_copy(ang[:, :], posi[:, :]))
            ang_step(dve.tensor_scalar(ang[:, :], ang[:, :], invs[:, 0:1], None, ALU.mult))
            ang_step(dve.tensor_scalar(kk[:, :], ang[:, :], 1.0 / two_pi, None, ALU.mult))
            ang_step(dve.tensor_scalar(kk[:, :], kk[:, :], 12582912.0, None, ALU.add))
            ang_step(dve.tensor_scalar(kk[:, :], kk[:, :], 12582912.0, None, ALU.subtract))
            for cpart in (c1, c2, c3):
                ang_step(dve.scalar_tensor_tensor(out=ang[:, :], in0=kk[:, :], scalar=-cpart, in1=ang[:, :],
                                                  op0=ALU.mult, op1=ALU.add))
            dve.tensor_scalar(kk[:, :], ang[:, :], pi, -pi, ALU.min, ALU.max).then_inc(S("ang_ready"), 1)
            ang_step(dve.tensor_scalar(ang[:, :], ang[:, :], float(np.pi / 2), None, ALU.add))
            ang_step(dve.tensor_scalar(ropc[:, :], ang[:, :], pi, -two_pi, ALU.is_gt, ALU.mult))
            ang_step(dve.tensor_tensor(ang[:, :], ang[:, :], ropc[:, :], ALU.add))
            dve.tensor_scalar(ang[:, :], ang[:, :], pi, -pi, ALU.min, ALU.max).then_inc(S("ang_ready"), 1)
            dve.wait_ge(S("sin_done"), 2)
            dve.tensor_scalar(rops[:, :], rops[:, :], invs[:, 1:2], None, ALU.mult).then_inc(S("rope_tables"), 1)

            front(0, 6, 8)
            dve.wait_ge(S("x_root"), 1)
            dve.reciprocal(rstd[:, :], rstd[:, :]).then_inc(S("x_inv"), 1)
            dve.wait_ge(S("x_inv"), 1)
            for g in range(NQ):
                if g == 2:
                    front(1, 0, 4)
                dve.tensor_tensor(xsq[:, KQ * g:KQ * g + KQ, :], xT[:, KQ * g:KQ * g + KQ, :],
                                  rstd[:, :].unsqueeze(1).broadcast_to([P, KQ, T]), ALU.mult).then_inc(S("x_normed"), 1)
            front(1, 4, 8)

            def read_sums(s, bank, n, total):
                dve.wait_ge(S("ada_sums"), total)
                dve.tensor_tensor(ada[:, s, :], ps[bank][:, 16 * n:16 * n + 16], bada[:, s, :], ALU.add)\
                   .then_inc(S("ada_read"), 1)

            def gain(name, dst, scale, which):
                dve.tensor_scalar(dst[:, :], ada[:, scale, :], 1.0, None, ALU.add).then_inc(S(name), 1)
                dve.wait_ge(S(name), 1)
                dve.tensor_tensor(dst[:, :], dst[:, :], gains[:, which, :], ALU.mult).then_inc(S(name), 1)

            read_sums(0, 1, 0, 1)
            for q in range(NQ):
                lo(dve, 0, 0, q)
            read_sums(1, 2, 0, 2)
            dve.wait_ge(S("ada_read"), 2)
            gain("h1_gain", a1, 1, 0)
            dve.wait_ge(S("h1_gain"), 2)
            dve.wait_ge(S("lb_step"), 7)
            dve.wait_ge(S("lam_ready"), 2)
            dve.wait_ge(S("rope_tables"), 1)

            def norms(h):
                dve.wait_ge(S("o_root"), h + 1)
                dve.reciprocal(sm[:, 24:28], sm[:, 20:24]).then_inc(S("o_inv"), 1)
                dve.wait_ge(S("o_inv"), h + 1)
                for k, dst in enumerate((on, oan)):
                    for t in range(TT):
                        dve.tensor_scalar(dst[:, t, :], ps[6][:, k * T + t * P:k * T + (t + 1) * P],
                                          sm[:, 24 + 2 * k + t:25 + 2 * k + t], None, ALU.mult).then_inc(S("on_ready"), 1)

            def outputs(h):
                dve.wait_ge(S("g_sig"), h + 1)
                dve.tensor_tensor(hg[:, :], hg[:, :], heg[:, :], ALU.mult).then_inc(S("g_silu"), 1)
                dve.wait_ge(S("oa_hi"), h + 1)
                dve.scalar_tensor_tensor(out=at(oalo, h), in0=ps[7][:, T:2 * T], scalar=vnorm[:, 0:1],
                                         in1=at(oahi, h).bitcast(F32), op0=ALU.mult, op1=ALU.subtract).then_inc(S("oa_lo"), 1)
                dve.wait_ge(S("g_silu"), h + 1)
                dve.scalar_tensor_tensor(out=obv[:, :], in0=ps[7][:, 0:T], scalar=vnorm[:, 1:2], in1=hg[:, :],
                                         op0=ALU.mult, op1=ALU.mult).then_inc(S("obv_ready"), 1)

            def hgrn_lo(h):
                dve.wait_ge(S("ob_hi"), h + 1)
                dve.tensor_tensor(at(oblo, h), obv[:, :], at(obhi, h).bitcast(F32), ALU.subtract).then_inc(S("ob_lo"), 1)

            def head(h, first):
                def chunk(j, qs=range(4)):
                    for q in qs:
                        if first and j == 0:
                            if q >= 2:
                                dve.wait_ge(S("h1_lo"), q - 1)
                            for k in range(KQ):
                                n = KQ * q + k
                                dve.tensor_scalar(hr[:, q % 2, k, :], xsq[:, n, :], a1[:, n:n + 1], ada[:, 0, n:n + 1],
                                                  ALU.mult, ALU.add).then_inc(S("h1_made"), 1)
                            dve.wait_ge(S("h1_made"), KQ * q + KQ)
                            dve.wait_ge(S("h1_hi"), KQ * q + KQ)
                            dve.tensor_tensor(hlo[:, KQ * q:KQ * q + KQ, :], hr[:, q % 2, :, :],
                                              hhi[:, KQ * q:KQ * q + KQ, :].bitcast(F32), ALU.subtract)\
                               .then_inc(S("h1_lo"), 1)
                        else:
                            lo(dve, main_pos(j), 12 * h + j, q)
                        if first and j == 0 and q == 3:
                            dve.wait_ge(S("acc_zero"), 4)
                        if j % 2 == 0 and q == 3:
                            n = j // 2
                            ada_chunk(dve, MAIN_C0, MAIN_K, h, 3 * n + 1, acc[:, n // 2, :],
                                      cs[:, bass.ds(2 * h + n % 2, 1)])

                chunk(0, (0, 1))
                if not first:
                    norms(h - 1)
                chunk(0, (2, 3))
                chunk(1)
                if not first:
                    outputs(h - 1)
                dve.wait_ge(S("evac"), 12 * h + HQ + 3)
                dve.tensor_tensor(hq[:, :], hq[:, :], he[:, :], ALU.mult).then_inc(S("q_silu"), 1)
                chunk(2)
                if not first:
                    hgrn_lo(h - 1)
                chunk(3)
                dve.wait_ge(S("evac"), 12 * h + FB + 3)
                for d in range(2):
                    dve.tensor_scalar(fF[:, d, :], fE[:, d, :], lbm[:, d, bass.ds(h, 1)], lb[:, d, bass.ds(h, 1)],
                                      ALU.mult, ALU.add).then_inc(S("f_made"), 1)
                dve.wait_ge(S("f_made"), 2 * h + 2)
                dve.tensor_scalar(fK[:, :, :], fF[:, :, :], -1.0, 1.0, ALU.mult, ALU.add).then_inc(S("f_ready"), 1)
                chunk(4)
                dve.wait_ge(S("logf"), h + 1)
                dve.tensor_tensor_scan(fE[:, 0, :], scanm[:, :], fF[:, 0, :], 0.0, ALU.mult, ALU.add)\
                   .then_inc(S("scanned"), 1)
                dve.tensor_tensor_scan(fE[:, 1, ::-1], scanm[:, :], fF[:, 1, ::-1], 0.0, ALU.mult, ALU.add)\
                   .then_inc(S("scanned"), 1)
                dve.wait_ge(S("scanned"), 2 * h + 2)
                for d in range(2):
                    b = fE[:, d, :].rearrange("p (c l) -> p c l", l=L)
                    mid = L // 2 - 1 if d == 0 else L // 2
                    end = L - 1 if d == 0 else 0
                    wide = lambda v: v.broadcast_to([P, NC, L])
                    dve.tensor_tensor(fM[:, d, :].rearrange("p (c l) -> p c l", l=L), b, wide(b[:, :, mid:mid + 1]),
                                      ALU.subtract).then_inc(S("b_diff"), 1)
                    dve.tensor_tensor(fL[:, d, :].rearrange("p (c l) -> p c l", l=L), wide(b[:, :, end:end + 1]), b,
                                      ALU.subtract).then_inc(S("b_diff"), 1)
                chunk(5, (0, 1, 2))
                q2 = hq[:, :].unsqueeze(1).broadcast_to([P, 2, T])
                dve.wait_ge(S("e_b"), h + 1)
                dve.wait_ge(S("q_silu"), h + 1)
                dve.tensor_tensor(fL[:, :, :], fL[:, :, :], fK[:, :, :], ALU.mult).then_inc(S("hg_fac"), 1)
                dve.tensor_tensor(fM[:, :, :], fM[:, :, :], fK[:, :, :], ALU.mult).then_inc(S("hg_fac"), 1)
                dve.tensor_tensor(fF[:, :, :], fF[:, :, :], q2, ALU.mult).then_inc(S("hg_fac"), 1)
                for d in range(2):
                    end = L - 1 if d == 0 else 0
                    dve.tensor_copy(dec[:, d, :], fE[:, d, :].rearrange("p (c l) -> p c l", l=L)[:, :, end:end + 1]
                                    .rearrange("p c l -> p (c l)")).then_inc(S("hg_fac"), 1)
                chunk(5, (3,))
                dve.wait_ge(S("hg_fac"), 5 * h + 5)
                dve.tensor_tensor(fE[:, :, :], fE[:, :, :], q2, ALU.mult).then_inc(S("qe_ready"), 1)
                chunk(6)
                chunk(7, (0, 1))
                tab = lambda v: v[:, :].unsqueeze(1).broadcast_to([P, 2, T])
                dve.wait_ge(S("rot_done"), h + 1)
                dve.tensor_tensor(ro[:, :, :], ps[7][:, :].rearrange("p (a n) -> p a n", a=2), tab(rops), ALU.mult)\
                   .then_inc(S("rope_chain"), 1)
                dve.tensor_tensor(qk[:, :, :], qk[:, :, :], tab(ropc), ALU.mult).then_inc(S("rope_chain"), 1)
                dve.wait_ge(S("rope_chain"), 2 * h + 2)
                dve.tensor_tensor(qk[:, :, :], qk[:, :, :], ro[:, :, :], ALU.add).then_inc(S("roped"), 1)
                chunk(7, (2, 3))
                dve.wait_ge(S("u_done"), h + 1)
                dve.wait_ge(S("qe_ready"), h + 1)
                for n in range(3):
                    for d in range(2):
                        c = n if d == 0 else NC - 1 - n
                        u = u_ps(c, d)
                        if n == 0:
                            ins = dve.tensor_copy(st[:, d, 0, :], u)
                        else:
                            dve.wait_ge(S("st_ready"), 6 * h + 2 * n + d - 1)
                            ins = dve.scalar_tensor_tensor(out=st[:, d, n, :], in0=st[:, d, n - 1, :],
                                                           scalar=dec[:, d, c:c + 1], in1=u, op0=ALU.mult, op1=ALU.add)
                        ins.then_inc(S("st_ready"), 1)
                chunk(8)
                dve.wait_ge(S("scores"), h + 1)
                for m in range(2):
                    dve.tensor_reduce(sm[:, m:4:2], sc_ps[m][:, :].rearrange("p (t k) -> p t k", t=TT), AX, ALU.max)\
                       .then_inc(S("rowmax"), 1)
                dve.wait_ge(S("rowmax"), 2 * h + 2)
                dve.tensor_scalar(sm[:, 0:4], sm[:, 0:4], -0.125, None, ALU.mult).then_inc(S("smax"), 1)
                chunk(9)
                dve.wait_ge(S("p_exp"), 4 * h + 4)
                dve.reciprocal(sm[:, 8:12], sm[:, 4:8]).then_inc(S("z_inv"), 1)
                dve.wait_ge(S("z_inv"), h + 1)
                dve.tensor_scalar(sm[:, 12:14], sm[:, 9:12:2], lam[:, 0:1], None, ALU.mult).then_inc(S("z_lam"), 1)
                dve.wait_ge(S("z_lam"), h + 1)
                for t in range(TT):
                    dve.tensor_scalar(pr[:, t, 1, :], pr[:, t, 1, :], sm[:, 12 + t:13 + t], None, ALU.mult)\
                       .then_inc(S("p1_scaled"), 1)
                for t in range(TT):
                    dve.wait_ge(S("p1_scaled"), 2 * h + t + 1)
                    dve.scalar_tensor_tensor(out=pr[:, t, 0, :], in0=pr[:, t, 0, :], scalar=sm[:, 8 + 2 * t:9 + 2 * t],
                                             in1=pr[:, t, 1, :], op0=ALU.mult, op1=ALU.add).then_inc(S("p_ready"), 1)
                chunk(10)
                chunk(11)

            loop(dve, HEADS, head)
            norms(HEADS - 1)
            outputs(HEADS - 1)
            hgrn_lo(HEADS - 1)
            read_sums(2, 2, 0, 4)
            read_sums(4, 2, 1, 4)
            dve.wait_ge(S("ada_read"), 4)
            gain("h2_gain", a2, 4, 1)

            def y_raw(n_w, slot, n, count):
                multiplied(dve, n_w)
                g = sg[:, bass.ds(n, 1), :, :].rearrange("p a b t -> p (a b t)")
                m = bm[:, slot, :, :].rearrange("p b t -> p (b t)")
                dve.tensor_tensor(m, ps[slot][:, :], g, ALU.mult).then_inc(S("z_read"), 1)
                dve.wait_ge(S("z_read"), count + 2)
                dve.tensor_tensor(yv[:, slot, :], bm[:, slot, 0, :], bm[:, slot, 1, :], ALU.add)\
                   .then_inc(S("y_ready_raw"), 1)

            def y_low(slot, n, count):
                dve.wait_ge(S("y_hi"), count)
                dve.tensor_tensor(at(hlo, n), yv[:, slot, :], at(hhi, n).bitcast(F32), ALU.subtract).then_inc(S("y_lo"), 1)

            def branch(i, first):
                for j in range(2):
                    for q in range(NQ):
                        lo(dve, j, BR_W0 + 2 * i + j, q)
                        if q == 1 and not (first and j == 0) and not (first and j == 1):
                            n = 2 * i + j - 2
                            y_low(j, n, n + 1)
                    n = 2 * i + j - 1
                    if not (first and j == 0):
                        y_raw(BR_W0 + n, 1 - j, n, n + 1)
            dve.wait_ge(S("gates_done"), HEADS)
            loop(dve, 8, branch)
            y_low(0, 14, 15)

            def residual(n_w, slot, n):
                multiplied(dve, n_w)
                dve.scalar_tensor_tensor(out=at(xT, n), in0=ps[slot][:, 0:T], scalar=ada[:, 2, bass.ds(n, 1)],
                                         in1=at(xT, n), op0=ALU.mult, op1=ALU.add).then_inc(S("x1_ready"), 1)

            def w_out(i, first):
                for j in range(4):
                    for q in range(NQ):
                        lo(dve, main_pos(j), WO_W0 + 4 * i + j, q)
                        if first and j == 0 and q == 1:
                            y_raw(BR_W0 + 15, 1, 15, 16)
                        if first and j == 0 and q == 2:
                            y_low(1, 15, 16)
                    if not (first and j == 0):
                        residual(WO_W0 + 4 * i + j - 1, (j - 1) % 2, 4 * i + j - 1)
                    if j % 2 == 0:
                        if first and j == 0:
                            dve.wait_ge(S("acc_zero"), 5)
                        ada_chunk(dve, WO_C0, 6, i, main_pos(j) + 1, acc[:, 0, :], cs[:, bass.ds(2 * i + j // 2, 1)])
            loop(dve, 4, w_out)
            for q in range(NQ):
                if q == 3:
                    residual(WO_W0 + 15, 1, 15)
                lo(dve, 0, WQ_W0, q)
            dve.wait_ge(S("x1_root"), 1)
            dve.reciprocal(rstd[:, :], rstd[:, :]).then_inc(S("x1_inv"), 1)
            dve.wait_ge(S("x1_inv"), 1)
            dve.wait_ge(S("h2_gain"), 2)

            for q in range(NQ):
                tiles = range(KQ * q, KQ * q + KQ)
                buf = lambda n: hr2[:, (n // KQ) % 2, n % KQ, :]
                for n in tiles:
                    if n >= 2 * KQ:
                        dve.wait_ge(S("h2_lo"), n - 2 * KQ + 1)
                    dve.scalar_tensor_tensor(out=buf(n), in0=xT[:, n, :], scalar=a2[:, n:n + 1], in1=rstd[:, :],
                                             op0=ALU.mult, op1=ALU.mult).then_inc(S("h2_normed"), 1)
                if q == 0:
                    read_sums(3, 3, 0, 5)
                for n in tiles:
                    dve.wait_ge(S("h2_hi"), n + 1)
                    dve.scalar_tensor_tensor(out=hlo[:, n, :], in0=buf(n), scalar=ada[:, 3, n:n + 1],
                                             in1=hhi[:, n, :].bitcast(F32), op0=ALU.add, op1=ALU.subtract)\
                       .then_inc(S("h2_lo"), 1)

            def query(i, first):
                for j in range(4):
                    for q in range(NQ):
                        if not (first and j == 0):
                            lo(dve, main_pos(j), WQ_W0 + 4 * i + j, q)
                    if j % 2 == 0:
                        ada_chunk(dve, WQ_C0, 6, i, main_pos(j) + 1, acc[:, 0, :], cs[:, bass.ds(2 * i + (8 + j // 2), 1)])
            loop(dve, 4, query)
            read_sums(5, 3, 0, 6)

            pairs = [(t, m) for t in range(TT) for m in range(2)]
            flat = [cand[:, t, :, :].rearrange("p a b -> p (a b)") for t in range(TT)]

            def route(n, k):
                if k == 0:
                    dve.wait_ge(S("sc_ready"), n + 1)
                    apart(dve)
                    for t, m in pairs:
                        dve.max(vals[:, t, m, 0:8], sc[:, t, m, :]).then_inc(S("top_a"), 1)
                elif k == 1:
                    dve.wait_ge(S("top_a"), 4 * n + 4)
                    apart(dve)
                    for t, m in pairs:
                        dve.match_replace(scw[:, t, m, :], vals[:, t, m, 0:8], sc[:, t, m, :], NEG).then_inc(S("top_b"), 1)
                elif k == 2:
                    for t, m in pairs:
                        dve.max_index(idx[:, t, m, 0:8], vals[:, t, m, 0:8], sc[:, t, m, :]).then_inc(S("top_i"), 1)
                elif k == 3:
                    dve.wait_ge(S("top_b"), 4 * n + 4)
                    apart(dve)
                    for t, m in pairs:
                        dve.max(vals[:, t, m, 8:16], scw[:, t, m, :]).then_inc(S("top_c"), 1)
                elif k == 4:
                    dve.wait_ge(S("top_c"), 4 * n + 4)
                    apart(dve)
                    for t, m in pairs:
                        dve.max_index(idx[:, t, m, 8:16], vals[:, t, m, 8:16], scw[:, t, m, :]).then_inc(S("top_i"), 1)
                elif k == 5:
                    for t in range(TT):
                        dve.tensor_tensor(cand[:, t, :, :], vals[:, t, 0, :].unsqueeze(2).broadcast_to([P, TOPK, TOPK]),
                                          vals[:, t, 1, :].unsqueeze(1).broadcast_to([P, TOPK, TOPK]), ALU.add)\
                           .then_inc(S("cand_made"), 1)
                    dve.wait_ge(S("top_i"), 8 * n + 8)
                    dve.tensor_copy(idf[:, :, :, :], idx[:, :, :, :]).then_inc(S("idf_made"), 1)
                elif k == 6:
                    dve.wait_ge(S("cand_made"), 2 * n + 2)
                    apart(dve)
                    for t in range(TT):
                        dve.max(cv[:, t, 0:8], flat[t]).then_inc(S("best_a"), 1)
                elif k == 7:
                    dve.wait_ge(S("best_a"), 2 * n + 2)
                    apart(dve)
                    for t in range(TT):
                        dve.match_replace(candw[:, t, :], cv[:, t, 0:8], flat[t], NEG).then_inc(S("best_b"), 1)
                elif k == 8:
                    for t in range(TT):
                        dve.max_index(ci[:, t, 0:8], cv[:, t, 0:8], flat[t]).then_inc(S("best_i"), 1)
                elif k == 9:
                    dve.wait_ge(S("best_b"), 2 * n + 2)
                    apart(dve)
                    for t in range(TT):
                        dve.max(cv[:, t, 8:16], candw[:, t, :]).then_inc(S("best_c"), 1)
                elif k == 10:
                    dve.wait_ge(S("best_c"), 2 * n + 2)
                    for t in range(TT):
                        dve.tensor_scalar(zn[:, t:t + 1], cv[:, t, 0:1], -1.0, None, ALU.mult).then_inc(S("zn_ready"), 1)
                    for t in range(TT):
                        dve.max_index(ci[:, t, 8:16], cv[:, t, 8:16], candw[:, t, :]).then_inc(S("best_i"), 1)
                elif k == 11:
                    dve.wait_ge(S("best_i"), 4 * n + 4)
                    dve.tensor_scalar(cj[:, :, 0, :], ci[:, :, :], 4, None, ALU.logical_shift_right).then_inc(S("cj_made"), 1)
                    dve.tensor_scalar(cj[:, :, 1, :], ci[:, :, :], 15, None, ALU.bitwise_and).then_inc(S("cj_made"), 1)
                elif k == 12:
                    dve.wait_ge(S("cj_made"), 2 * n + 2)
                    for t in range(TT):
                        dve.tensor_copy(cjf[:, t, :, :], cj[:, t, :, :]).then_inc(S("cj_ready"), 1)
                elif k in (13, 14):
                    t = k - 13
                    dve.wait_ge(S("cj_ready"), 2 * n + t + 1)
                    o = oneh[:, t, :, :].rearrange("p s (k j) -> p s k j", j=TOPK)
                    dve.tensor_tensor(o, cjf[:, t, :, :].unsqueeze(3).broadcast_to([P, 2, TOPK, TOPK]),
                                      iota[:, 0:TOPK].unsqueeze(1).unsqueeze(1).broadcast_to([P, 2, TOPK, TOPK]),
                                      ALU.is_equal).then_inc(S("oneh_made"), 1)
                elif k == 15:
                    dve.wait_ge(S("cg_exp"), 2 * n + 2)
                    dve.reciprocal(zr[:, :], zs[:, :]).then_inc(S("zr_made"), 1)
                elif k == 16:
                    dve.wait_ge(S("zr_made"), n + 1)
                    for t in range(TT):
                        dve.tensor_scalar(at3(eit[:, 2, t], n), cg[:, t, :], zr[:, t:t + 1], None, ALU.mult)\
                           .then_inc(S("eit_ready"), 1)
                elif k in (18, 19):
                    t = k - 18
                    dve.wait_ge(S("picked"), 2 * n + t + 1)
                    for m in range(2):
                        ins = dve.tensor_reduce(at3(eit[:, m, t], n), oneh[:, t, m, :].rearrange("p (k j) -> p k j", j=TOPK),
                                                AX, ALU.add)
                        ins.then_inc(S("eit_ready"), 1)
                elif k == 20:
                    dve.wait_ge(S("eit_ready"), 6 * n + 6)
                    dve.sem_inc(S("sc_used"), 1)

            with dve.Fori(0, HEADS) as i:
                for j in range(ROUTE_K):
                    for q in range(NQ):
                        lo(dve, j, U_W0 + ROUTE_K * i + j, q)
                        route(i, 4 * j + q)
            dve.wait_ge(S("egT_ready"), 2)
            with dve.Fori(0, (REST_AT - GATE_AT) // 2) as i:
                for j in range(2):
                    for q in range(NQ):
                        lo(dve, j, U_W0 + GATE_AT + 2 * i + j, q)
                        if q % 2 == 0:
                            g = 2 * j + q // 2
                            dve.wait_ge(S("g_made"), 4 * i + g + 1)
                            for t in range(2):
                                e1, e2, gt = [egT[:, n, bass.ds(8 * i + 2 * g + t, 1)] for n in range(3)]
                                dve.tensor_scalar(o12[:, g % 2, 0, t, :], iota[:, :], e1, gt, ALU.is_equal, ALU.mult)\
                                   .then_inc(S("onehots"), 1)
                                dve.tensor_scalar(o12[:, g % 2, 1, t, :], iota[:, :], e2, None, ALU.is_equal)\
                                   .then_inc(S("onehots"), 1)
            with dve.Fori(0, (NKEYS - REST_AT) // 2) as i:
                for j in range(2):
                    for q in range(NQ):
                        lo(dve, j, U_W0 + REST_AT + 2 * i + j, q)

            def table_v(i, first):
                for j in range(2):
                    if first and j == 0:
                        dve.wait_ge(S("g_copied"), 130)
                    dve.wait_ge(S(f"s_back{j}"), 16 * i + 16)
                    g = G[:, :, bass.ds(2 * i + j, 1)].rearrange("p t a -> p (t a)")
                    dve.tensor_tensor(av[:, j, :], sld[:, j, :], g, ALU.mult).then_inc(S("a_made"), 1)
                    lo(dve, j, V_W0 + 2 * i + j, 0)
                    lo(dve, j, V_W0 + 2 * i + j, 1)
                    dve.wait_ge(S("a_hi"), 2 * i + j + 1)
                    dve.tensor_tensor(alo[:, j, :], av[:, j, :], ahi[:, j, :].bitcast(F32), ALU.subtract)\
                       .then_inc(S("a_lo"), 1)
                    lo(dve, j, V_W0 + 2 * i + j, 2)
                    lo(dve, j, V_W0 + 2 * i + j, 3)
            loop(dve, 64, table_v)

            dve.wait_ge(S("x1_back"), 16)
            dve.wait_ge(S("ada_read"), 6)
            for n in range(KT):
                dve.wait_ge(pe_read, 4 * (V_W0 + 127) + n // KQ + 5)
                dve.scalar_tensor_tensor(out=x1[:, n, :], in0=ps[n // 2][:, (n % 2) * T:(n % 2 + 1) * T],
                                         scalar=ada[:, 5, n:n + 1], in1=x1[:, n, :], op0=ALU.mult, op1=ALU.add)\
                   .then_inc(S("x2_ready"), 1)
            dve.wait_ge(S("x2_root"), 1)
            dve.reciprocal(rstde[:, :], rstde[:, :]).then_inc(S("x2_inv"), 1)
            dve.wait_ge(S("x2_inv"), 1)
            for g in range(NQ):
                dve.wait_ge(S("x2_scaled"), KQ * g + KQ)
                dve.tensor_tensor(x1[:, KQ * g:KQ * g + KQ, :], x1[:, KQ * g:KQ * g + KQ, :],
                                  rstde[:, :].unsqueeze(1).broadcast_to([P, KQ, T]), ALU.mult).then_inc(S("y_ready"), 1)


def constants():
    p = np.arange(P)
    r = p % 64
    inv = np.power(np.float32(500000.0), -np.arange(0, ROPE, 2, dtype=np.float32) / np.float32(ROPE)).astype(np.float32)
    half = ROPE // 2
    perm = np.zeros((P, P), np.float32)
    for n in range(P):
        if r[n] < ROPE:
            perm[n + half if r[n] < half else n - half, n] = 1.0
    freq = np.where(r < ROPE, inv[r % half], 0.0).astype(np.float32)
    sign = np.where(r < half, -1.0, 1.0).astype(np.float32)
    scan = np.broadcast_to((np.arange(T) % L != 0).astype(np.float32), (P, T))
    return {"ident": np.eye(P, dtype=np.float32), "perm": perm,
            "iota": np.broadcast_to(np.arange(P, dtype=np.float32), (P, P)),
            "scanm": scan, "inv": np.stack([freq, sign], 1)}


def kernel(**inputs):
    import concourse.bacc as bacc
    from concourse.bass_utils import run_bass_kernel_spmd as run

    x = {n: np.asarray(v) for n, v in inputs.items()}
    cols = lambda v: v.reshape(-1, P).T
    chunks = lambda w: w.reshape(-1, P, w.shape[1] // P, P).transpose(2, 1, 0, 3).reshape(w.shape[1] // P, P, -1)
    wide = lambda v: np.broadcast_to(v, (P,) + v.shape)
    lbt = np.stack([x["hgrn_lb_fwd"], x["hgrn_lb_bwd"]]).reshape(2, 2, HEADS, P).transpose(3, 0, 1, 2)
    arrays = {
        "xT": x["x"][0].T.reshape(KT, P, T).transpose(1, 0, 2),
        "cT": cols(x["c"][0]),
        "posi": wide(x["positions"][0]),
        "w_ada": x["w_ada"][0],
        "b_ada": x["b_ada"][0].reshape(6, KT, P).transpose(2, 0, 1),
        "gains": np.stack([cols(x["norm1_g"][0]), cols(x["norm2_g"][0]), cols(x["final_norm_g"])], 1),
        "w_in": chunks(x["w_in"][0]),
        "lqk": wide(np.stack([x["diff_lq1"][0], x["diff_lk1"][0], x["diff_lq2"][0], x["diff_lk2"][0]])),
        "vnorm": np.stack([x["diff_subln_g"][0], x["hgrn_norm_g"][0]], 1),
        "lbt": lbt,
        "w_br": np.concatenate([chunks(x["w_branch_attn"][0]), chunks(x["w_branch_hgrn"][0])], 2),
        "w_out": chunks(x["w_out"][0]),
        "wq": chunks(x["peer_wq"][0]),
        "keys": np.stack([x["peer_keys1"][0], x["peer_keys2"][0]]).transpose(3, 0, 1, 2),
        "u": x["peer_u"][0].reshape(NKEYS, NKEYS, KT, P).transpose(1, 3, 2, 0).reshape(NKEYS, P, KT * P),
        "v": x["peer_v"][0],
    }
    arrays.update(constants())
    arrays = {n: np.ascontiguousarray(v) for n, v in arrays.items()}
    nc = bacc.Bacc("TRN2", target_bir_lowering=False, num_devices=1)
    aps = {n: nc.dram_tensor(n + "_dram", v.shape, mybir.dt.from_np(v.dtype), kind="ExternalInput").ap()
           for n, v in arrays.items()}
    x1_keep = nc.dram_tensor("x1_keep", (P, KT * T), F32, kind="Internal").ap()
    s_keep = nc.dram_tensor("s_keep", (NKEYS, P, T), F32, kind="Internal").ap()
    out = nc.dram_tensor("out_dram", (P, KT * T), F32, kind="ExternalOutput").ap()
    layer(nc, aps, x1_keep, s_keep, out)
    r = run(nc, [{n + "_dram": v for n, v in arrays.items()}], core_ids=[0])
    y = r.results[0]["out_dram"].reshape(P, KT, T).transpose(2, 1, 0).reshape(1, T, D)
    return np.ascontiguousarray(y)
```
